# Optimizing a Trainium2 kernel written in Bass

```python
import math
import jax, jax.numpy as jnp
from jax import lax
import numpy as np

D_MODEL = 1024
BATCH = 1
SEQ = 512
DEPTH = 1

N_META = 16
RET_HEADS = 4
RET_QK_HEAD = 128
RET_V_HEAD = 256
RET_CHUNK = 128
ROPE_BASE = 10000.0
HY_WIDTH = D_MODEL
HY_SHORT_CONV = 3
HY_EMB_DIM = 33
HY_FILTER_ORDER = 64
HY_FAST_DECAY_PCT = 0.3
HY_SLOW_DECAY_PCT = 1.5
HY_DECAY_TARGET = 1e-2
N_EXPERTS = 16
EC_CAPACITY = 2
D_FF_EXPERT = 2 * D_MODEL
RMS_EPS = 1e-6

RET_QK_W = RET_HEADS * RET_QK_HEAD
RET_V_W = RET_HEADS * RET_V_HEAD
IN_SPLITS = (RET_QK_W, RET_QK_W, RET_V_W, RET_V_W, 3 * HY_WIDTH, D_MODEL, D_MODEL)
IN_PROJ_W = sum(IN_SPLITS)

kernel_name = 'hybrid_retention_hyena_ecmoe_encoder'

def rms_norm(x, g):
    xf = x.astype(jnp.float32)
    y = xf * lax.rsqrt(jnp.mean(xf * xf, axis=-1, keepdims=True) + RMS_EPS)
    return (y * g.astype(jnp.float32)).astype(x.dtype)

def rotary(x, pos):
    half = x.shape[-1] // 2
    inv = ROPE_BASE ** (-jnp.arange(half, dtype=jnp.float32) / half)
    ang = pos[:, None] * inv[None, :]
    cos = jnp.cos(ang)[:, None, :].astype(x.dtype)
    sin = jnp.sin(ang)[:, None, :].astype(x.dtype)
    x1, x2 = x[..., :half], x[..., half:]
    return jnp.concatenate([x1 * cos - x2 * sin, x1 * sin + x2 * cos], axis=-1)

def bidir_retention(q, k, v, log_gf, log_gb):
    B, T, H, _ = q.shape
    dt = q.dtype
    C = RET_CHUNK
    pad = (-T) % C
    n = (T + pad) // C

    def to_chunks(a):
        a = jnp.pad(a, ((0, 0), (pad, 0), (0, 0), (0, 0)))
        return a.reshape(B, n, C, H, a.shape[-1]).transpose(0, 3, 1, 2, 4)

    qc, kc, vc = to_chunks(q), to_chunks(k), to_chunks(v)
    i = jnp.arange(C, dtype=jnp.float32)
    diff = i[:, None] - i[None, :]
    lf = log_gf[:, None, None]
    lb = log_gb[:, None, None]
    mask = jnp.exp(jnp.where(diff >= 0, lf * diff, -lb * diff)).astype(dt)
    scores = jnp.einsum('bhncd,bhned->bhnce', qc, kc) * mask[None, :, None]
    intra = jnp.einsum('bhnce,bhned->bhncd', scores, vc)

    w_end = jnp.exp(log_gf[:, None] * (C - 1 - i)[None, :]).astype(dt)
    w_start = jnp.exp(log_gb[:, None] * i[None, :]).astype(dt)
    a_f = jnp.einsum('bhncd,hc,bhnce->nbhde', kc, w_end, vc)
    a_b = jnp.einsum('bhncd,hc,bhnce->nbhde', kc, w_start, vc)
    dec_f = jnp.exp(log_gf * C).astype(dt)
    dec_b = jnp.exp(log_gb * C).astype(dt)

    def states(a, dec, reverse):
        def step(s, a_n):
            return s * dec[None, :, None, None] + a_n, s
        _, ss = lax.scan(step, jnp.zeros_like(a[0]), a, reverse=reverse)
        return ss

    s_f = states(a_f, dec_f, False)
    s_b = states(a_b, dec_b, True)
    qw_f = jnp.exp(log_gf[:, None] * (i + 1.0)[None, :]).astype(dt)
    qw_b = jnp.exp(log_gb[:, None] * (C - i)[None, :]).astype(dt)
    cross = (jnp.einsum('bhncd,hc,nbhde->bhnce', qc, qw_f, s_f)
             + jnp.einsum('bhncd,hc,nbhde->bhnce', qc, qw_b, s_b))
    o = (intra + cross).transpose(0, 2, 3, 1, 4).reshape(B, n * C, H, -1)
    return o[:, pad:]

def head_rms_norm(o, g):
    of = o.astype(jnp.float32)
    y = of * lax.rsqrt(jnp.mean(of * of, axis=-1, keepdims=True) + RMS_EPS)
    return (y * g.astype(jnp.float32).reshape(o.shape[2], o.shape[3])).astype(o.dtype)

def short_conv_centred(u, w, b):
    T = u.shape[1]
    half = HY_SHORT_CONV // 2
    up = jnp.pad(u, ((0, 0), (half, half), (0, 0)))
    return sum(up[:, j:j + T] * w[j] for j in range(HY_SHORT_CONV)) + b

def hyena_filters(T, w1, b1, w2, b2, w3, b3, freq, w4):
    f32 = jnp.float32
    t = jnp.arange(T, dtype=f32)
    t_norm = t / (T - 1)
    bands = (HY_EMB_DIM - 1) // 2
    fr = jnp.linspace(1e-4, bands - 1, bands, dtype=f32)
    ang = (2.0 * math.pi * t / T)[:, None] * fr[None, :]
    feat = jnp.concatenate([t_norm[:, None], jnp.cos(ang), -jnp.sin(ang)], axis=-1)
    fq = freq.astype(f32)
    hdn = jnp.sin(fq * (feat @ w1.astype(f32) + b1.astype(f32)))
    hdn = jnp.sin(fq * (hdn @ w2.astype(f32) + b2.astype(f32)))
    hdn = jnp.sin(fq * (hdn @ w3.astype(f32) + b3.astype(f32)))
    filt = (hdn @ w4.astype(f32)).reshape(T, 2, HY_WIDTH)
    max_decay = math.log(HY_DECAY_TARGET) / HY_FAST_DECAY_PCT
    min_decay = math.log(HY_DECAY_TARGET) / HY_SLOW_DECAY_PCT
    deltas = jnp.linspace(min_decay, max_decay, HY_WIDTH, dtype=f32)
    window = jnp.exp(-t_norm[:, None] * jnp.abs(deltas)[None, :])
    filt = filt * window[:, None, :]
    return filt[:, 0], filt[:, 1]

def bidir_fftconv(z, h_f, h_b):
    T = z.shape[1]
    n = 2 * T
    g = jnp.concatenate([h_f, jnp.zeros((1, h_f.shape[1]), jnp.float32), h_b[:0:-1]], axis=0)
    zf = jnp.fft.rfft(z.astype(jnp.float32), n=n, axis=1)
    gf = jnp.fft.rfft(g, n=n, axis=0)
    y = jnp.fft.irfft(zf * gf[None], n=n, axis=1)[:, :T]
    return y.astype(z.dtype)

def expert_choice_moe(xn, w_router, w_gate, w_up, w_down):
    B, T, _ = xn.shape
    cap = EC_CAPACITY * T // N_EXPERTS
    logits = jnp.einsum('btd,de->bte', xn, w_router).astype(jnp.float32)
    aff = jax.nn.softmax(logits, axis=-1)
    gate, idx = lax.top_k(jnp.swapaxes(aff, 1, 2), cap)
    bidx = jnp.arange(B)[:, None, None]
    xe = xn[bidx, idx]
    hid = jax.nn.silu(jnp.einsum('becd,edf->becf', xe, w_gate)) * jnp.einsum('becd,edf->becf', xe, w_up)
    ye = jnp.einsum('becf,efd->becd', hid, w_down) * gate[..., None].astype(xn.dtype)
    return jnp.zeros_like(xn).at[bidx, idx].add(ye)

def setup_inputs(seed: int = 0) -> dict:
    key = jax.random.key(seed)
    ks = iter(jax.random.split(key, 40))
    f32 = jnp.float32
    L = DEPTH

    def nrm(shape, scale):
        return jax.random.normal(next(ks), shape, f32) * scale

    hh = jnp.arange(RET_HEADS, dtype=f32)
    decay_base = jnp.log(2.0 ** (5.0 + hh) - 1.0)
    return {
        'x': nrm((BATCH, SEQ, D_MODEL), 1.0),
        'meta_tokens': nrm((N_META, D_MODEL), 1.0),
        'norm1_g': 1.0 + nrm((L, D_MODEL), 0.01),
        'w_in': nrm((L, D_MODEL, IN_PROJ_W), D_MODEL ** -0.5),
        'ret_decay_fwd': decay_base[None] + nrm((L, RET_HEADS), 0.1),
        'ret_decay_bwd': decay_base[None] + nrm((L, RET_HEADS), 0.1),
        'ret_head_norm_g': 1.0 + nrm((L, RET_V_W), 0.01),
        'w_ret_out': nrm((L, RET_V_W, D_MODEL), RET_V_W ** -0.5),
        'hy_conv_w': nrm((L, HY_SHORT_CONV, 3 * HY_WIDTH), HY_SHORT_CONV ** -0.5),
        'hy_conv_b': nrm((L, 3 * HY_WIDTH), 0.01),
        'hy_filt_w1': nrm((L, HY_EMB_DIM, HY_FILTER_ORDER), HY_EMB_DIM ** -0.5),
        'hy_filt_b1': nrm((L, HY_FILTER_ORDER), 0.01),
        'hy_filt_w2': nrm((L, HY_FILTER_ORDER, HY_FILTER_ORDER), HY_FILTER_ORDER ** -0.5),
        'hy_filt_b2': nrm((L, HY_FILTER_ORDER), 0.01),
        'hy_filt_w3': nrm((L, HY_FILTER_ORDER, HY_FILTER_ORDER), HY_FILTER_ORDER ** -0.5),
        'hy_filt_b3': nrm((L, HY_FILTER_ORDER), 0.01),
        'hy_filt_freq': 1.0 + nrm((L, HY_FILTER_ORDER), 0.01),
        'hy_filt_w4': nrm((L, HY_FILTER_ORDER, 2 * HY_WIDTH), 0.1 * HY_FILTER_ORDER ** -0.5),
        'hy_skip': nrm((L, HY_WIDTH), 1.0),
        'w_hy_out': nrm((L, HY_WIDTH, D_MODEL), HY_WIDTH ** -0.5),
        'w_o': nrm((L, D_MODEL, D_MODEL), D_MODEL ** -0.5),
        'norm2_g': 1.0 + nrm((L, D_MODEL), 0.01),
        'w_router': nrm((L, D_MODEL, N_EXPERTS), D_MODEL ** -0.5),
        'w_exp_gate': nrm((L, N_EXPERTS, D_MODEL, D_FF_EXPERT), D_MODEL ** -0.5),
        'w_exp_up': nrm((L, N_EXPERTS, D_MODEL, D_FF_EXPERT), D_MODEL ** -0.5),
        'w_exp_down': nrm((L, N_EXPERTS, D_FF_EXPERT, D_MODEL), D_FF_EXPERT ** -0.5),
        'final_norm_g': 1.0 + nrm((D_MODEL,), 0.01),
    }

def reference(x, meta_tokens, norm1_g, w_in, ret_decay_fwd, ret_decay_bwd, ret_head_norm_g, w_ret_out,
              hy_conv_w, hy_conv_b, hy_filt_w1, hy_filt_b1, hy_filt_w2, hy_filt_b2, hy_filt_w3, hy_filt_b3,
              hy_filt_freq, hy_filt_w4, hy_skip, w_hy_out, w_o, norm2_g, w_router, w_exp_gate, w_exp_up,
              w_exp_down, final_norm_g):
    B = x.shape[0]
    meta = jnp.broadcast_to(meta_tokens[None].astype(x.dtype), (B, N_META, D_MODEL))
    h = jnp.concatenate([meta, x], axis=1)
    T = h.shape[1]
    pos = jnp.arange(T, dtype=jnp.float32)
    offs = np.cumsum(IN_SPLITS)[:-1].tolist()
    for l in range(DEPTH):
        xn = rms_norm(h, norm1_g[l])
        proj = xn @ w_in[l]
        q, k, v, g_ret, u_hy, gate_a, gate_b = jnp.split(proj, offs, axis=-1)

        q = rotary(q.reshape(B, T, RET_HEADS, RET_QK_HEAD), pos)
        k = rotary(k.reshape(B, T, RET_HEADS, RET_QK_HEAD), pos) * (RET_QK_HEAD ** -0.5)
        v = v.reshape(B, T, RET_HEADS, RET_V_HEAD)
        o = bidir_retention(q, k, v,
                            jax.nn.log_sigmoid(ret_decay_fwd[l].astype(jnp.float32)),
                            jax.nn.log_sigmoid(ret_decay_bwd[l].astype(jnp.float32)))
        o = head_rms_norm(o, ret_head_norm_g[l]).reshape(B, T, RET_V_W)
        y_a = (jax.nn.silu(g_ret) * o) @ w_ret_out[l]

        uc = short_conv_centred(u_hy, hy_conv_w[l], hy_conv_b[l])
        x0, x1, vh = jnp.split(uc, 3, axis=-1)
        h_f, h_b = hyena_filters(T, hy_filt_w1[l], hy_filt_b1[l], hy_filt_w2[l], hy_filt_b2[l],
                                 hy_filt_w3[l], hy_filt_b3[l], hy_filt_freq[l], hy_filt_w4[l])
        z = x1 * vh
        y_b = (x0 * (bidir_fftconv(z, h_f, h_b) + z * hy_skip[l])) @ w_hy_out[l]

        mixed = jax.nn.sigmoid(gate_a) * y_a + jax.nn.sigmoid(gate_b) * y_b
        h = h + mixed @ w_o[l]

        h = h + expert_choice_moe(rms_norm(h, norm2_g[l]), w_router[l], w_exp_gate[l],
                                  w_exp_up[l], w_exp_down[l])
    return rms_norm(h, final_norm_g)[:, N_META:]


_drawn_inputs = setup_inputs


def setup_inputs(seed=0):
    import zlib

    import numpy as np

    out = dict(_drawn_inputs(seed))
    spreads = {}
    factors = {'norm1_g': 4.359,
     'ret_head_norm_g': 64.0,
     'hy_conv_b': 5.168,
     'hy_filt_b1': 8.0,
     'hy_filt_b2': 8.0,
     'hy_filt_b3': 8.0,
     'hy_filt_freq': 8.0,
     'norm2_g': 40.832,
     'final_norm_g': 31.413}
    for name, (base, spread) in spreads.items():
        noise = np.random.default_rng([zlib.crc32(name.encode()), seed]).standard_normal(out[name].shape)
        drawn = base * np.exp(spread * noise) if base else spread * noise
        out[name] = __import__('jax').numpy.asarray(drawn.astype(out[name].dtype))
    for name, factor in factors.items():
        out[name] = (out[name] * factor).astype(out[name].dtype)
    return out
```

```python
from contextlib import ExitStack

import concourse.bass as bass
from concourse import mybir

F32 = mybir.dt.float32
F16 = mybir.dt.float16
U32 = mybir.dt.uint32
ALU = mybir.AluOpType
ACT = mybir.ActivationFunctionType
AX_X = mybir.AxisListType.X

D, SEQ, NMETA, HEADS, DK, DV = 1024, 512, 16, 4, 128, 256
T = SEQ + NMETA
E, FF = 16, 2048
CAP = 2 * T // E
ROUNDS = -(-CAP // 8)
GR = -(-CAP // 32)
EPS = 1e-6
KD = D // 128
TS = [(0, NMETA)] + [(NMETA + 128 * i, 128) for i in range(SEQ // 128)]
NT = len(TS)
CUT = TS[3][0]
P0 = 512 - CUT
CW = 256
HALF = 512
UW = TS[-1][0] + T
U0 = TS[-1][0]

W_S = 2.0 ** 8
Z_S = 2.0 ** -2
F_S = 2.0 ** 6
G_S = 2.0 ** -8
YA_S = 2.0 ** -4
YB_S = 2.0 ** -6
MIX_S = 2.0 ** -4
MAGIC = 1.5 * 2.0 ** 23
TWO_PI = 6.283185307179586
PI_HI = 6.28125
PI_LO = TWO_PI - PI_HI
PI_IN = 3.1415925

C_G1, C_RG, C_CW, C_CB, C_SK, C_DF, C_DB, C_WR, N_PAR = 0, 8, 16, 88, 112, 120, 124, 128, 256
C_TOK, C_EPS, N_CON = 0, 5, 8
F_W1, F_W2, F_W3, F_B, F_FQ, N_FP = 0, 64, 128, 192, 195, 196


def chunk_list():
    out = []
    for hf in range(2):
        for part in (1, 2, 0):
            out += [("w_in", 3072 + D * part + HALF * hf + CW * c) for c in range(2)]
    out += [("w_in", CW * c) for c in range(4)]
    out += [("w_in", 1024 + CW * c) for c in range(4)]
    out += [("w_in", 2048 + CW * c) for c in range(4)]
    for c in range(4):
        out += [("w_in", 6144 + CW * c), ("w_ret_out", CW * c)]
    for c in range(4):
        out += [("w_in", 7168 + CW * c), ("w_hy_out", CW * c)]
    out += [("w_o", CW * c) for c in range(4)]
    return out


CHUNKS = chunk_list()
NCH = len(CHUNKS)
C_Q, C_V, C_GR, C_A, C_B, C_O = 12, 16, 20, 24, 32, 40
MOE_CH = 12
SLOTS = 6


def job_list():
    jobs = []

    def add(name, sem, count):
        jobs.append((name, sem, count))

    u = 0
    add(("H", 0), "filt_arg", 1)
    for j in range(KD):
        add(("X", j), "x_split", j + 1)
    for hf in range(2):
        for part in range(3):
            for i in range(4):
                u += 1
                add(("U", hf, part, i), "u_evac", 2 * u)
                if hf == 0 and part == 0 and i in (1, 3):
                    add(("H", (i + 1) // 2), "filt_arg", 1 + (i + 1) // 2)
            if part == 0:
                for k in range(NT):
                    add(("FL", hf, k), "filt_win", hf * NT + k + 1)
            if part == 1:
                for f in range(NT):
                    add(("G", hf, f), "g_evac", hf * NT + f + 1)
                for k in range(NT):
                    add(("ZT", hf, k), "zt_split", hf * NT + k + 1)
                for f in range(NT):
                    add(("Z", hf, f), "z_mul", hf * NT + f + 1)
                for i in range(4):
                    add(("Y", hf, i), "y_done", hf * 4 + i + 1)
    for i in range(8):
        add(("QK", i), "rot_mul", i + 1)
    for c in range(4):
        for k in range(NT):
            add(("V", c, k), "v_evac", c * NT + k + 1)
    for h in range(HEADS + 1):
        if h < HEADS:
            for k in range(NT):
                add(("S", h, k), "sc_ready", h * NT + k + 1)
        if h >= 1:
            for j in range(2):
                add(("O", h - 1, j), "sq_ready", 2 * (2 * (h - 1) + j) + 2)
            add(("N", h - 1), "rms_root", h)
    for j in range(KD):
        add(("GR", j), "silu_ready", j + 1)
    for c in range(4):
        for i in range(2):
            add(("GA", 2 * c + i), "gate_ready", 2 * c + i + 1)
        for i in range(2):
            add(("YA", 2 * c + i), "mix_a", 2 * c + i + 1)
    for c in range(4):
        for i in range(2):
            add(("GB", 2 * c + i), "gate_ready", KD + 2 * c + i + 1)
        for i in range(2):
            add(("YB", 2 * c + i), "mix_b", 2 * c + i + 1)
    for c in range(4):
        for k in range(NT):
            add(("WO", c, k), "h_add", c * NT + k + 1)
    for j in range(KD):
        add(("XT", j), "xt_evac", j + 1)
    add(("L",), "logits_in", 2)
    add(("AT",), "work_in", 1)
    add(("C",), "cols_in", 1)
    for i in range(2):
        add(("R", i), "idx_row", i + 1)
    return jobs


JOBS = job_list()
AT = {name: n for n, (name, _, _) in enumerate(JOBS)}
NJ = len(JOBS)
LAST_JOB = []
for _n in range(NCH):
    if _n < C_Q:
        _hf, _r = divmod(_n, 6)
        _part, _c = divmod(_r, 2)
        LAST_JOB.append(AT[("U", _hf, _part, 2 * _c + 1)])
    elif _n < C_V:
        LAST_JOB.append(AT[("QK", 2 * (_n - C_Q) + 1)])
    elif _n < C_GR:
        LAST_JOB.append(AT[("V", _n - C_V, NT - 1)])
    elif _n < C_A:
        LAST_JOB.append(AT[("GR", 2 * (_n - C_GR) + 1)])
    elif _n < C_O:
        _g = "GA" if _n < C_B else "GB"
        _c, _o = divmod(_n - (C_A if _n < C_B else C_B), 2)
        LAST_JOB.append(AT[(("YA" if _n < C_B else "YB") if _o else _g, 2 * _c + 1)])
    else:
        LAST_JOB.append(AT[("WO", _n - C_O, NT - 1)])

SEMS = ("consts filt_params dft_fwd dft_inv win tables rows2 h_tok h_again g_rows moe_consts out_stored "
        "rms1_sq rms1_root rms1_inv hs_ready x_hi x_split border conv_w "
        "raw_hi raw_lo tile_done filt_arg filt_red sin_ready "
        "u_evac u_step u_used filt_win filt_sum filt_hi filt_lo g_evac z_ready zt_hi zt_split "
        "z_skip z_mul p_sum p_hi p_lo y_done yb_prod yb_hi yb_split "
        "dec_exp dec_ln dec_neg mask_arg mask_ready rot_mul rot_a rot_ready v_evac sc_ready sq_ready rms_root rms_inv "
        "silu_ready og_ready yain_prod yain_hi yain_split gate_ready mix_a mix_b mix_sum mix_hi mix_split h_add "
        "rms2_sq rms2_root rms2_inv xn2_ready xt_evac lg_zero logits_in lg_sub lg_exp lg_aff work_in "
        "idx_found xn2_hi xn2_lo cols_in blk_ready idx_row sel_ready xe_done xcur_pad chain "
        "xcur_ready chunk_used st_ready silu_g hid_ready hidt_done hidt_ready ye_act ye_dve scat_done moe_add "
        "fin_sq fin_root fin_inv fin_ready").split()


def build(nc, A, out):
    ctx = ExitStack()
    with ctx:
        base = (nc.sbuf_base + 63) // 64 * 64
        SM, XN, YA, YB = 0, 4096, 4096 + 21120, 4096 + 2 * 21120
        RAW = YB + 16896
        SPL = RAW + 24576
        TOP = SPL + 24576
        END = TOP + SLOTS * 16384
        ctx.enter_context(nc.sbuf_tensor("arena", [128, (END + base - nc.sbuf_base) // 4 + 8], F32))

        def sb(name, shape, dt, off):
            return nc.alloc_sbuf_tensor_at(name, shape, dt, offset=base + off)

        S = {n: ctx.enter_context(nc.semaphore("s_" + n)) for n in SEMS}
        raw_in = [ctx.enter_context(nc.semaphore(f"s_raw_in{i}")) for i in range(3)]
        slot_in = [ctx.enter_context(nc.semaphore(f"s_slot_in{i}")) for i in range(SLOTS)]
        ps_all = ctx.enter_context(nc.psum_tensor("ps_all", [128, 4096], F32))

        par = sb("par", [128, N_PAR], F32, SM)
        con = sb("con", [128, N_CON], F32, SM + 1024)
        ident = sb("ident", [128, 128], F32, SM + 1056)
        ones = sb("ones", [128, 128], F32, SM + 1568)
        cw = sb("cw", [128, 24], F32, SM + 2080)
        ss = sb("ss", [128, 8], F32, SM + 2176)
        root = sb("root", [128, 8], F32, SM + 2208)
        rinv = sb("rinv", [128, 8], F32, SM + 2240)
        dec = sb("dec", [128, 32], F32, SM + 2272)
        rgs = sb("rgs", [128, 8], F32, SM + 2400)
        lgs = sb("lgs", [128, NT, E], F32, SM + 2432)
        lmax = sb("lmax", [128, NT], F32, SM + 2752)
        lsum = sb("lsum", [128, NT], F32, SM + 2784)
        vals = sb("vals", [E, 8 * ROUNDS], F32, SM + 2816)
        idxu = sb("idxu", [E, 8 * ROUNDS], U32, SM + 3104)
        idxf = sb("idxf", [E, 8 * ROUNDS], F32, SM + 3392)
        cols = sb("cols", [CAP, 2 * E], F32, SM + 3904)
        xnt = sb("xnt", [128, KD, 2, T], F16, XN)
        xn2 = sb("xn2", [128, NT, D], F32, XN)
        dft_f = sb("dft_f", [128, NT, 4, T], F16, YA)
        yain = sb("yain", [128, KD, 2, T], F16, YA)
        h = sb("h", [128, NT, D], F32, YA)
        ybin = sb("ybin", [128, KD, 2, T], F16, YB)
        xn2t = sb("xn2t", [128, KD, T], F32, YB)
        st = sb("st", [CAP, SEQ], F32, YB)
        ye = sb("ye", [CAP, D], F32, YB + 2048)
        junk2 = sb("junk2", [128, D], F32, YB + 2048 + 4096)
        hidt = sb("hidt", [128, GR, 4, 128], F32, YB + 2048 + 8192)
        xcur = sb("xcur", [128, KD, 32 * GR], F32, XN)
        sel = sb("sel", [128, NT, CAP], F16, XN + 3072)
        hid = sb("hid", [128, GR, 512], F32, XN + 4096)
        hg = sb("hg", [128, GR, 512], F32, XN + 4096 + 6144)
        raw = [sb(f"raw{i}", [128, KD, CW], F32, RAW + 8192 * i) for i in range(3)]
        wsp = [sb(f"wsp{i}", [128, 2, KD, CW], F16, SPL + 8192 * i) for i in range(3)]
        g2b = sb("g2b", [128, D], F32, RAW)
        gfb = sb("gfb", [128, D], F32, RAW + 4096)
        iota = sb("iota", [128, T], F32, RAW + 8192)
        idxb = sb("idxb", [128, E * CAP], F32, RAW + 10304)
        blk = sb("blk", [E, E * CAP], F32, RAW + 14528)
        blki = sb("blki", [E, E, CAP], F32, RAW + 18752)
        xn2p = sb("xn2p", [128, NT, 2, D], F16, SPL)
        work = sb("work", [E, T], F32, SPL + 20480)
        slot = [sb(f"slot{i}", [128, 4096], F32, TOP + 16384 * i) for i in range(SLOTS)]
        upad = [sb(f"upad{i}", [128, T + 2], F32, TOP + 2144 * i) for i in range(2)]
        acc = [sb(f"acc{i}", [128, T], F32, TOP + 4288 + 2112 * i) for i in range(2)]
        zt_c = sb("zt_c", [128, 4, T], F32, TOP + 8512)
        fp_ = sb("filt_sum_parts", [128, NT, 2, HALF], F16, TOP + 16960)
        fm_ = sb("filt_dif_parts", [128, NT, 2, HALF], F16, TOP + 27200)
        zt_t = sb("zt_t", [128, NT, 2, HALF], F16, TOP + 16960)
        htok = sb("htok", [128, NT, D], F32, TOP + 16960)
        gsp = sb("gsp", [128, NT, 2, HALF], F32, TOP + 37440)
        psp = sb("psp", [128, NT, 4, HALF], F16, TOP + 37440)
        win = sb("win_t", [128, NT, HALF], F32, TOP + 37440)
        feat = sb("feat", [33, T], F32, TOP + 37440 + 10240)
        fpar = sb("fpar", [64, N_FP], F32, TOP + 37440 + 12352)
        hdn = sb("hdn", [64, T], F32, TOP + 57920)
        w4 = sb("w4", [64, 2 * D], F32, TOP + 60032)
        dft_i = sb("dft_i", [128, NT, 4, T], F16, TOP + 68224)
        tmp = [sb(f"tmp{i}", [128, HALF], F32, TOP + 89344 + 2048 * i) for i in range(4)]
        farg = sb("farg", [64, T], F32, TOP + 89344)
        frnd = sb("frnd", [64, T], F32, TOP + 89344 + 2112)
        junk = sb("junk", [128, D], F32, TOP + 89344 + 4224 - 4224)
        rot = [sb(f"rot{i}", [128, T], F32, TOP + 8512 + 2112 * i) for i in range(2)]
        sqb = sb("sqb", [128, 2, T], F32, TOP + 12736)
        rs = sb("rs", [128, HEADS, T], F32, TOP)
        cosT = sb("cosT", [128, T], F32, TOP + 16960)
        sinT = sb("sinT", [128, T], F32, TOP + 19072)
        utab = sb("utab", [128, UW], F32, TOP + 21184)
        mask = sb("mask", [128, HEADS, UW], F32, TOP + 24896)
        qk = sb("qk", [128, 8, T], F32, TOP + 39744)
        v = sb("v", [128, NT, D], F32, TOP + 56640)
        sc = [sb(f"sc{i}", [128, NT, T], F32, TOP + 77120 + 10560 * i) for i in range(2)]
        marg = [sb(f"marg{i}", [128, UW], F32, TOP + 77120 + 3712 * i) for i in range(2)]
        mix32 = sb("mix32", [128, KD, T], F32, TOP + 65536)
        mixp = sb("mixp", [128, KD, 2, T], F16, TOP + 65536)
        sgt = [sb(f"sgt{i}", [128, T], F32, TOP + 82432 + 2112 * i) for i in range(2)]
        tb = [sb(f"tb{i}", [128, T], F32, TOP + 86656 + 2112 * i) for i in range(2)]

        def pair(n, a=0, b=1024, p=128):
            q = n % 4
            return ps_all[0:p, 1024 * q + a:1024 * q + b]

        def full(n, p0=0, p1=128):
            q = n % 4
            return ps_all[p0:p1, 1024 * q + P0:1024 * q + P0 + T]

        def dram(ap):
            return ap

        w = {k: A[k][0].rearrange("(k p) n -> p k n", p=128) for k in ("w_in", "w_ret_out", "w_hy_out", "w_o")}
        w_gate, w_up, w_down = A["w_exp_gate"][0], A["w_exp_up"][0], A["w_exp_down"][0]

        def moe_src(e, c):
            if c < 8:
                q = c % 4
                m = w_gate if c < 4 else w_up
                return m[e].rearrange("(p k) n -> p k n", k=KD)[:, 2 * q:2 * q + 2, :]
            return w_down[e].rearrange("(j p s) n -> j p s n", j=4, s=4)[c - 8]

        def moe_dst(c):
            s = slot[c % SLOTS][:, :]
            return s.rearrange("p (k n) -> p k n", k=2 if c < 8 else 4)

        block = ctx.enter_context(nc.Block())

        @block.sync
        def _(sp):
            sp.dma_start(htok[0:NMETA, 0, :], A["meta_tokens"]).then_inc(S["h_tok"], 16)
            sp.dma_start(htok[:, 1:NT, :], A["x"][0].rearrange("(k p) d -> p k d", p=128)).then_inc(S["h_tok"], 16)

            def load_chunk(n):
                if n >= 3:
                    sp.wait_ge(S["raw_lo"], n - 2)
                name, c0 = CHUNKS[n]
                sp.dma_start(raw[n % 3][:, :, :], w[name][:, :, c0:c0 + CW]).then_inc(raw_in[n % 3], 16)

            def load_first(c):
                sp.dma_start(moe_dst(c), moe_src(0, c)).then_inc(slot_in[c], 16)

            for n in range(NCH):
                load_chunk(n)
                if n == 1:
                    sp.dma_start(w4[:, :], A["hy_filt_w4"][0]).then_inc(S["filt_params"], 16)
                    sp.dma_start(win[:, :, :], A["c_win"][:, :, 0, :]).then_inc(S["win"], 16)
                    sp.dma_start(dft_f[:, :, :, :], A["c_dft_f"]).then_inc(S["dft_fwd"], 16)
                    sp.dma_start(dft_i[:, :, :, :], A["c_dft_i"]).then_inc(S["dft_inv"], 16)
                if n == 7:
                    sp.wait_ge(S["tile_done"], AT[("Y", 0, 3)] + 1)
                    sp.dma_start(win[:, :, :], A["c_win"][:, :, 1, :]).then_inc(S["win"], 16)
                if n == 12:
                    sp.wait_ge(S["tile_done"], AT[("Z", 1, NT - 1)] + 1)
                    sp.dma_start(cosT[:, :], A["c_cos"]).then_inc(S["tables"], 16)
                    sp.dma_start(sinT[:, :], A["c_sin"]).then_inc(S["tables"], 16)
                    sp.dma_start(utab[:, :], A["c_u"]).then_inc(S["tables"], 16)
                if n >= C_A + 1 and n < C_A + 5:
                    if n == C_A + 1:
                        sp.wait_ge(S["yain_split"], KD)
                    load_first(n - C_A - 1)
                if n == C_B + 2:
                    sp.wait_ge(S["tile_done"], AT[("YA", KD - 1)] + 1)
                    sp.dma_start(h[0:NMETA, 0, :], A["meta_tokens"]).then_inc(S["h_again"], 16)
                    sp.dma_start(h[:, 1:NT, :], A["x"][0].rearrange("(k p) d -> p k d", p=128)).then_inc(S["h_again"], 16)
            sp.wait_ge(S["raw_lo"], NCH)
            sp.dma_start(g2b[:, :], A["norm2_g"][0].partition_broadcast(128)).then_inc(S["g_rows"], 16)
            sp.dma_start(gfb[:, :], A["final_norm_g"].partition_broadcast(128)).then_inc(S["g_rows"], 16)
            sp.dma_start(iota[:, :], A["c_iota"]).then_inc(S["moe_consts"], 16)
            sp.dma_start(blk[:, :], A["c_blk"]).then_inc(S["moe_consts"], 16)
            sp.wait_ge(S["tile_done"], AT[("WO", 3, NT - 1)] + 1)
            load_first(4)
            load_first(5)

            def load(e, c, used):
                if c != 8:
                    sp.wait_ge(S["chunk_used"], used + 1 if c == 7 else used)
                sp.dma_start(moe_dst(c), moe_src(e, c)).then_inc(slot_in[c % SLOTS], 16)

            with sp.Fori(0, E - 1) as e:
                for c in range(SLOTS, MOE_CH):
                    load(e, c, e * MOE_CH + (c - SLOTS + 1))
                for c in range(SLOTS):
                    load(e + 1, c, e * MOE_CH + (c + SLOTS + 1))
            for c in range(SLOTS, MOE_CH):
                load(E - 1, c, (E - 1) * MOE_CH + c - SLOTS + 1)
            for k in range(1, NT):
                sp.wait_ge(S["fin_ready"], k)
                sp.dma_start(out[0, 128 * (k - 1):128 * k, :], h[:, k, :]).then_inc(S["out_stored"], 16)
            sp.wait_ge(S["out_stored"], 16 * (NT - 1))

        @block.gpsimd
        def _(pool):
            nc.gpsimd.memset(ones[:, :], 1.0).then_inc(S["border"], 1)
            for hf in range(2):
                for k in range(NT):
                    p = TS[k][1]
                    n = hf * NT + k
                    pool.wait_ge(S["filt_win"], n + 1)
                    if n:
                        pool.wait_ge(S["filt_lo"], 2 * n)
                        pool.wait_ge(S["filt_hi"], 2 * n)
                    nc.gpsimd.tensor_tensor(tmp[2][0:p, :], tmp[0][0:p, :], tmp[1][0:p, :], ALU.add).then_inc(S["filt_sum"], 1)
                    nc.gpsimd.tensor_tensor(tmp[3][0:p, :], tmp[0][0:p, :], tmp[1][0:p, :], ALU.subtract).then_inc(S["filt_sum"], 1)
                    for i, dst in enumerate((fp_, fm_)):
                        pool.wait_ge(S["filt_hi"], 2 * n + i + 1)
                        pool.wait_ge(S["filt_sum"], 2 * n + i + 1)
                        nc.gpsimd.tensor_tensor(dst[0:p, k, 1, :], tmp[2 + i][0:p, :], dst[0:p, k, 0, :], ALU.subtract).then_inc(S["filt_lo"], 1)
                pool.wait_ge(S["consts"], 48)
                pool.wait_ge(S["tile_done"], AT[("ZT", hf, NT - 1)] + 1)
                for i in range(4):
                    c = C_SK + 4 * hf + i
                    nc.gpsimd.tensor_scalar(zt_c[:, i, :], zt_c[:, i, :], par[:, c:c + 1], None, ALU.mult).then_inc(S["z_skip"], 1)
                for f in range(NT):
                    p = TS[f][1]
                    n = hf * NT + f
                    pool.wait_ge(S["z_mul"], n + 1)
                    nc.gpsimd.tensor_tensor(tmp[0][0:p, :], tmp[0][0:p, :], tmp[1][0:p, :], ALU.subtract).then_inc(S["p_sum"], 1)
                    nc.gpsimd.tensor_tensor(tmp[2][0:p, :], tmp[2][0:p, :], tmp[3][0:p, :], ALU.add).then_inc(S["p_sum"], 1)
                    for i in range(2):
                        pool.wait_ge(S["p_hi"], 2 * n + i + 1)
                        pool.wait_ge(S["p_sum"], 2 * n + i + 1)
                        nc.gpsimd.tensor_tensor(psp[0:p, f, 2 * i + 1, :], tmp[2 * i][0:p, :], psp[0:p, f, 2 * i, :], ALU.subtract).then_inc(S["p_lo"], 1)
            for i in range(8):
                pool.wait_ge(S["rot_mul"], i + 1)
                nc.gpsimd.tensor_tensor(qk[:, i, :], rot[0][:, :], rot[1][:, :], ALU.add).then_inc(S["rot_ready"], 1)

        @block.scalar
        def _(act):
            act.dma_start(par[:, :], A["p_par"]).then_inc(S["consts"], 16)
            act.dma_start(con[:, :], A["c_con"]).then_inc(S["consts"], 16)
            act.dma_start(ident[:, :], A["c_ident"]).then_inc(S["consts"], 16)
            act.dma_start(feat[:, :], A["c_feat"]).then_inc(S["filt_params"], 16)
            act.dma_start(fpar[:, :], A["p_filt"]).then_inc(S["filt_params"], 16)

            def raw_hi(n):
                if n >= NCH:
                    return
                act.wait_ge(raw_in[n % 3], 16 * (n // 3 + 1))
                if n >= 3:
                    act.wait_ge(S["tile_done"], LAST_JOB[n - 3] + 1)
                nc.scalar.activation(wsp[n % 3][:, 0, :, :], raw[n % 3][:, :, :], ACT.Copy, scale=W_S).then_inc(S["raw_hi"], 1)

            eps = con[:, C_EPS:C_EPS + 1]
            act.wait_ge(S["consts"], 48)
            act.wait_ge(S["h_tok"], 32)
            for k, (_, p) in enumerate(TS):
                if k:
                    act.wait_ge(S["rms1_sq"], k)
                nc.scalar.activation(junk[0:p, :], htok[0:p, k, :], ACT.Square, accum_out=ss[0:p, k:k + 1]).then_inc(S["rms1_sq"], 1)
            act.wait_ge(S["rms1_sq"], NT)
            nc.scalar.activation(root[:, 1:NT], ss[:, 1:NT], ACT.Sqrt, bias=eps, scale=1.0 / D).then_inc(S["rms1_root"], 1)
            nc.scalar.activation(root[0:NMETA, 0:1], ss[0:NMETA, 0:1], ACT.Sqrt, bias=eps[0:NMETA, :], scale=1.0 / D).then_inc(S["rms1_root"], 1)
            raw_hi(0)
            raw_hi(1)

            def sine(l):
                act.wait_ge(S["filt_red"], l + 1)
                nc.scalar.activation(hdn[:, :], farg[:, :], ACT.Sin).then_inc(S["sin_ready"], 1)

            def u_evac(u):
                hf, r = divmod(u, 12)
                part, i = divmod(r, 4)
                j = AT[("U", hf, (1, 2, 0).index((1, 2, 0)[part]), i)]
                ct = (8, 16, 0)[part] + 4 * hf + i
                act.wait_ge(S["tile_done"], j + 1)
                if u >= 2:
                    act.wait_ge(S["u_used"], u - 1)
                nc.scalar.activation(upad[u % 2][:, 1:T + 1], full(j), ACT.Copy, scale=1.0 / W_S).then_inc(S["u_evac"], 1)
                nc.scalar.activation(acc[u % 2][:, :], full(j), ACT.Identity, scale=cw[:, ct:ct + 1],
                                     bias=par[:, C_CB + ct:C_CB + ct + 1]).then_inc(S["u_evac"], 1)

            for j in range(KD):
                act.wait_ge(S["tile_done"], AT[("X", j)] + 1)
                nc.scalar.activation(xnt[:, j, 0, :], full(AT[("X", j)]), ACT.Copy,
                                     scale=par[:, C_G1 + j:C_G1 + j + 1]).then_inc(S["x_hi"], 1)
                if j == 1:
                    sine(0)
            act.wait_ge(S["conv_w"], 1)
            act.wait_ge(S["border"], 5)
            for hf in range(2):
                for part in range(3):
                    for c in range(2):
                        raw_hi(6 * hf + 2 * part + c + 2)
                        for i in (2 * c, 2 * c + 1):
                            u_evac(12 * hf + 4 * part + i)
                            if part == 2:
                                n = 4 * hf + i
                                act.wait_ge(S["yb_prod"], n + 1)
                                nc.scalar.activation(ybin[:, n, 0, :], acc[(12 * hf + 8 + i) % 2][:, :], ACT.Copy).then_inc(S["yb_hi"], 1)
                        if hf == 0 and part == 0:
                            sine(c + 1)
                    if part == 0:
                        for k in range(NT):
                            p, n = TS[k][1], hf * NT + k
                            for i, dst in enumerate((fp_, fm_)):
                                act.wait_ge(S["filt_sum"], 2 * n + i + 1)
                                nc.scalar.activation(dst[0:p, k, 0, :], tmp[2 + i][0:p, :], ACT.Copy).then_inc(S["filt_hi"], 1)
                    if part == 1:
                        for f in range(NT):
                            p, j = TS[f][1], AT[("G", hf, f)]
                            act.wait_ge(S["tile_done"], j + 1)
                            nc.scalar.activation(gsp[0:p, f, :, :].rearrange("p a n -> p (a n)"), pair(j, p=p), ACT.Copy,
                                                 scale=G_S).then_inc(S["g_evac"], 1)
                        for k in range(NT):
                            p, j = TS[k][1], AT[("ZT", hf, k)]
                            act.wait_ge(S["tile_done"], j + 1)
                            nc.scalar.activation(zt_t[0:p, k, 0, :], pair(j, 0, HALF, p), ACT.Copy, scale=Z_S).then_inc(S["zt_hi"], 1)
                        for f in range(NT):
                            p, n = TS[f][1], hf * NT + f
                            for i in range(2):
                                act.wait_ge(S["p_sum"], 2 * n + i + 1)
                                nc.scalar.activation(psp[0:p, f, 2 * i, :], tmp[2 * i][0:p, :], ACT.Copy).then_inc(S["p_hi"], 1)
            raw_hi(C_Q + 2)
            nc.scalar.activation(dec[:, 0:8], par[:, C_DF:C_DF + 8], ACT.Exp, scale=-1.0).then_inc(S["dec_exp"], 1)
            act.wait_ge(S["dec_exp"], 1)
            nc.scalar.activation(dec[:, 8:16], dec[:, 0:8], ACT.Ln, bias=ones[:, 0:1]).then_inc(S["dec_ln"], 1)
            for hh in range(HEADS):
                act.wait_ge(S["mask_arg"], hh + 1)
                nc.scalar.activation(mask[:, hh, :], marg[0][:, :], ACT.Exp).then_inc(S["mask_ready"], 1)
            for c in range(1, 4):
                raw_hi(C_Q + 2 + c)
            for c in range(4):
                raw_hi(C_V + 2 + c)
                for k in range(NT):
                    p, j = TS[k][1], AT[("V", c, k)]
                    act.wait_ge(S["tile_done"], j + 1)
                    nc.scalar.activation(v[0:p, k, CW * c:CW * c + CW], pair(j, 0, CW, p), ACT.Copy, scale=1.0 / W_S).then_inc(S["v_evac"], 1)
            for hh in range(HEADS):
                for j2 in range(2):
                    j = AT[("O", hh, j2)]
                    act.wait_ge(S["tile_done"], j + 1)
                    if hh:
                        act.wait_ge(S["tile_done"], AT[("N", hh - 1)] + 1)
                    nc.scalar.activation(qk[:, hh + 4 * j2, :], full(j), ACT.Copy).then_inc(S["sq_ready"], 1)
                    nc.scalar.activation(sqb[:, j2, :], full(j), ACT.Square).then_inc(S["sq_ready"], 1)
                j = AT[("N", hh)]
                act.wait_ge(S["tile_done"], j + 1)
                nc.scalar.activation(rs[:, hh, :], full(j), ACT.Sqrt, scale=1.0 / DV, bias=eps).then_inc(S["rms_root"], 1)
            for c in range(4):
                raw_hi(C_GR + 2 + c)
                for j in (2 * c, 2 * c + 1):
                    act.wait_ge(S["tile_done"], AT[("GR", j)] + 1)
                    if j >= 2:
                        act.wait_ge(S["yain_prod"], j - 1)
                    nc.scalar.activation(sgt[j % 2][:, :], full(AT[("GR", j)]), ACT.Silu, scale=1.0 / W_S).then_inc(S["silu_ready"], 1)
                    act.wait_ge(S["yain_prod"], j + 1)
                    nc.scalar.activation(yain[:, j, 0, :], tb[j % 2][:, :], ACT.Copy).then_inc(S["yain_hi"], 1)
            for c in range(4):
                raw_hi(C_A + 2 + 2 * c)
                for j in (2 * c, 2 * c + 1):
                    act.wait_ge(S["tile_done"], AT[("GA", j)] + 1)
                    if j >= 2:
                        act.wait_ge(S["mix_a"], j - 1)
                    nc.scalar.activation(sgt[j % 2][:, :], full(AT[("GA", j)]), ACT.Sigmoid, scale=1.0 / W_S).then_inc(S["gate_ready"], 1)
                raw_hi(C_A + 3 + 2 * c)
            for c in range(4):
                raw_hi(C_B + 2 + 2 * c)
                for j in (2 * c, 2 * c + 1):
                    act.wait_ge(S["tile_done"], AT[("GB", j)] + 1)
                    if j >= 2:
                        act.wait_ge(S["mix_b"], j - 1)
                    else:
                        act.wait_ge(S["mix_a"], KD)
                    nc.scalar.activation(sgt[j % 2][:, :], full(AT[("GB", j)]), ACT.Sigmoid, scale=1.0 / W_S).then_inc(S["gate_ready"], 1)
                raw_hi(C_B + 3 + 2 * c)
                for j in (2 * c, 2 * c + 1):
                    act.wait_ge(S["mix_sum"], j + 1)
                    nc.scalar.activation(mixp[:, j, 0, :], tb[j % 2][:, :], ACT.Copy).then_inc(S["mix_hi"], 1)
            raw_hi(C_O + 2)
            raw_hi(C_O + 3)
            for k, (_, p) in enumerate(TS):
                act.wait_ge(S["h_add"], 3 * NT + k + 1)
                if k:
                    act.wait_ge(S["rms2_sq"], k)
                nc.scalar.activation(junk2[0:p, :], h[0:p, k, :], ACT.Square, accum_out=ss[0:p, k:k + 1]).then_inc(S["rms2_sq"], 1)
                act.wait_ge(S["rms2_sq"], k + 1)
                nc.scalar.activation(root[0:p, k:k + 1], ss[0:p, k:k + 1], ACT.Sqrt, bias=eps[0:p, :], scale=1.0 / D).then_inc(S["rms2_root"], 1)
            for k, (_, p) in enumerate(TS):
                act.wait_ge(S["xn2_ready"], k + 1)
                if k == 0:
                    act.wait_ge(S["tile_done"], AT[("WO", 3, NT - 1)] + 1)
                nc.scalar.activation(xn2p[0:p, k, 0, :], xn2[0:p, k, :], ACT.Copy).then_inc(S["xn2_hi"], 1)
            for j in range(KD):
                act.wait_ge(S["tile_done"], AT[("XT", j)] + 1)
                nc.scalar.activation(xn2t[:, j, :], full(AT[("XT", j)]), ACT.Copy).then_inc(S["xt_evac"], 1)
            act.wait_ge(S["lg_sub"], 1)
            nc.scalar.activation(lgs[:, :, :], lgs[:, :, :], ACT.Exp).then_inc(S["lg_exp"], 1)

            def evac_x(e):
                act.wait_ge(S["xe_done"], e + 1)
                for b in range(2):
                    src = ps_all[:, 3072 + 512 * b:3072 + 512 * b + 4 * CAP].rearrange("p (k c) -> p k c", k=4)
                    nc.scalar.activation(xcur[:, 4 * b:4 * b + 4, 0:CAP], src, ACT.Copy).then_inc(S["xcur_ready"], 1)

            act.wait_ge(S["xcur_pad"], 1)
            evac_x(0)

            def moe(e, last):
                act.wait_ge(S["chunk_used"], e * MOE_CH + 4)
                nc.scalar.activation(hg[:, :, :].rearrange("p g n -> p (g n)"), ps_all[:, 0:512 * GR], ACT.Silu).then_inc(S["silu_g"], 1)
                if not last:
                    act.wait_ge(S["chunk_used"], e * MOE_CH + 8)
                    evac_x(e + 1)
                act.wait_ge(S["hidt_done"], e + 1)
                nc.scalar.activation(hidt[:, :, :, :].rearrange("p g s c -> p (g s c)"), ps_all[:, 0:512 * GR], ACT.Copy).then_inc(S["hidt_ready"], 1)
                act.wait_ge(S["chunk_used"], e * MOE_CH + 12)
                for g in range(GR):
                    r = min(32, CAP - 32 * g)
                    for nq in range(2):
                        nc.scalar.activation(ye[32 * g:32 * g + r, 256 * nq:256 * nq + 256],
                                             ps_all[32 * nq:32 * nq + r, 1536 + 512 * g:1792 + 512 * g], ACT.Copy).then_inc(S["ye_act"], 1)

            with act.Fori(0, E - 1) as e:
                moe(e, False)
            moe(E - 1, True)
            for k in range(1, NT):
                act.wait_ge(S["moe_add"], (E - 1) * 4 + k)
                if k > 1:
                    act.wait_ge(S["fin_sq"], k - 1)
                nc.scalar.activation(junk2[:, :], h[:, k, :], ACT.Square, accum_out=ss[:, k:k + 1]).then_inc(S["fin_sq"], 1)
                act.wait_ge(S["fin_sq"], k)
                nc.scalar.activation(root[:, k:k + 1], ss[:, k:k + 1], ACT.Sqrt, bias=eps, scale=1.0 / D).then_inc(S["fin_root"], 1)

        @block.vector
        def _(dve):
            chain = [0]

            def link(ins):
                chain[0] += 1
                ins.then_inc(S["chain"], 1)
                dve.wait_ge(S["chain"], chain[0])

            def raw_lo(n):
                if n >= NCH:
                    return
                dve.wait_ge(S["raw_hi"], n + 1)
                nc.vector.scalar_tensor_tensor(wsp[n % 3][:, 1, :, :], raw[n % 3][:, :, :], W_S, wsp[n % 3][:, 0, :, :],
                                               ALU.mult, ALU.subtract).then_inc(S["raw_lo"], 1)

            for i in range(2):
                nc.vector.memset(upad[i][:, 0:1], 0.0).then_inc(S["border"], 1)
                nc.vector.memset(upad[i][:, T + 1:T + 2], 0.0).then_inc(S["border"], 1)
            dve.wait_ge(S["consts"], 48)
            nc.vector.tensor_scalar(cw[:, :], par[:, C_CW + 24:C_CW + 48], 1.0 / W_S, None, ALU.mult).then_inc(S["conv_w"], 1)
            link(nc.vector.tensor_scalar(rgs[:, :], par[:, C_RG:C_RG + 8], YA_S, None, ALU.mult))
            dve.wait_ge(S["rms1_root"], 2)
            link(nc.vector.reciprocal(rinv[:, 1:NT], root[:, 1:NT]))
            link(nc.vector.reciprocal(rinv[0:NMETA, 0:1], root[0:NMETA, 0:1]))
            for k, (_, p) in enumerate(TS):
                nc.vector.tensor_scalar(htok[0:p, k, :], htok[0:p, k, :], rinv[0:p, k:k + 1], None, ALU.mult).then_inc(S["hs_ready"], 1)

            def filt_arg(l):
                j = AT[("H", l)]
                dve.wait_ge(S["tile_done"], j + 1)
                fq, b = fpar[:, F_FQ:F_FQ + 1], fpar[:, F_B + l:F_B + l + 1]
                if l == 0:
                    dve.wait_ge(S["filt_params"], 48)
                    dve.wait_ge(S["rms1_sq"], NT)
                else:
                    dve.wait_ge(S["sin_ready"], l)
                nc.vector.tensor_scalar(farg[:, :], full(j, 0, 64), b, fq, ALU.add, ALU.mult).then_inc(S["filt_arg"], 1)
                dve.wait_ge(S["filt_arg"], l + 1)
                link(nc.vector.tensor_scalar(frnd[:, :], farg[:, :], 1.0 / TWO_PI, MAGIC, ALU.mult, ALU.add))
                link(nc.vector.tensor_scalar(frnd[:, :], frnd[:, :], MAGIC, None, ALU.subtract))
                link(nc.vector.scalar_tensor_tensor(farg[:, :], frnd[:, :], -PI_HI, farg[:, :], ALU.mult, ALU.add))
                link(nc.vector.scalar_tensor_tensor(farg[:, :], frnd[:, :], -PI_LO, farg[:, :], ALU.mult, ALU.add))
                nc.vector.tensor_scalar(farg[:, :], farg[:, :], PI_IN, -PI_IN, ALU.min, ALU.max).then_inc(S["filt_red"], 1)

            for j in range(KD):
                if j == 1:
                    filt_arg(0)
                dve.wait_ge(S["x_hi"], j + 1)
                nc.vector.scalar_tensor_tensor(xnt[:, j, 1, :], full(AT[("X", j)]), par[:, C_G1 + j:C_G1 + j + 1],
                                               xnt[:, j, 0, :], ALU.mult, ALU.subtract).then_inc(S["x_split"], 1)
                if j < 2:
                    raw_lo(j)

            def conv(u):
                hf, r = divmod(u, 12)
                part, i = divmod(r, 4)
                ct = (8, 16, 0)[part] + 4 * hf + i
                w0, w2 = (par[:, C_CW + 24 * t + ct:C_CW + 24 * t + ct + 1] for t in (0, 2))
                up, ac = upad[u % 2], acc[u % 2]
                dve.wait_ge(S["u_evac"], 2 * u + 2)
                link(nc.vector.scalar_tensor_tensor(ac[:, :], up[:, 0:T], w0, ac[:, :], ALU.mult, ALU.add))
                if part == 0:
                    nc.vector.scalar_tensor_tensor(zt_c[:, i, :], up[:, 2:T + 2], w2, ac[:, :], ALU.mult, ALU.add).then_inc(S["u_used"], 1)
                    return
                link(nc.vector.scalar_tensor_tensor(ac[:, :], up[:, 2:T + 2], w2, ac[:, :], ALU.mult, ALU.add))
                if part == 1:
                    dve.wait_ge(S["u_used"], 12 * hf + i + 1)
                    nc.vector.tensor_tensor(zt_c[:, i, :], zt_c[:, i, :], ac[:, :], ALU.mult).then_inc(S["u_used"], 1)
                else:
                    n = 4 * hf + i
                    dve.wait_ge(S["y_done"], n + 1)
                    nc.vector.scalar_tensor_tensor(ac[:, :], ac[:, :], YB_S, zt_c[:, i, :], ALU.mult, ALU.mult).then_inc(S["yb_prod"], 1)
                    dve.wait_ge(S["yb_hi"], n + 1)
                    nc.vector.tensor_tensor(ybin[:, n, 1, :], ac[:, :], ybin[:, n, 0, :], ALU.subtract).then_inc(S["u_used"], 1)

            for hf in range(2):
                for part in range(3):
                    for c in range(2):
                        raw_lo(6 * hf + 2 * part + c + 2)
                        for i in (2 * c, 2 * c + 1):
                            conv(12 * hf + 4 * part + i)
                        if hf == 0 and part == 0:
                            filt_arg(c + 1)
                    if part == 0:
                        dve.wait_ge(S["win"], 16 * (hf + 1))
                        if hf == 0:
                            dve.wait_ge(S["sin_ready"], 3)
                        for k in range(NT):
                            p, n, j = TS[k][1], hf * NT + k, AT[("FL", hf, k)]
                            dve.wait_ge(S["tile_done"], j + 1)
                            if n:
                                dve.wait_ge(S["filt_sum"], 2 * n)
                            if k == 0 and hf:
                                dve.wait_ge(S["p_lo"], 2 * n)
                            link(nc.vector.tensor_tensor(tmp[0][0:p, :], pair(j, 0, 512, p), win[0:p, k, :], ALU.mult))
                            if k == 0:
                                link(nc.vector.tensor_tensor(tmp[1][0:p, :], pair(j, 512, 1024, p), win[0:p, k, :], ALU.mult))
                                nc.vector.memset(tmp[1][0:1, :], 0.0).then_inc(S["filt_win"], 1)
                            else:
                                nc.vector.tensor_tensor(tmp[1][0:p, :], pair(j, 512, 1024, p), win[0:p, k, :], ALU.mult).then_inc(S["filt_win"], 1)
                    if part == 1:
                        for k in range(NT):
                            p, n, j = TS[k][1], hf * NT + k, AT[("ZT", hf, k)]
                            dve.wait_ge(S["zt_hi"], n + 1)
                            nc.vector.scalar_tensor_tensor(zt_t[0:p, k, 1, :], pair(j, 0, HALF, p), Z_S, zt_t[0:p, k, 0, :],
                                                           ALU.mult, ALU.subtract).then_inc(S["zt_split"], 1)
                        dve.wait_ge(S["filt_lo"], 2 * NT * (hf + 1))
                        dve.wait_ge(S["filt_hi"], 2 * NT * (hf + 1))
                        dve.wait_ge(S["g_evac"], NT * (hf + 1))
                        for f in range(NT):
                            p, n, j = TS[f][1], hf * NT + f, AT[("Z", hf, f)]
                            dve.wait_ge(S["tile_done"], j + 1)
                            if f:
                                dve.wait_ge(S["p_lo"], 2 * n)
                            for t, (a, b) in enumerate(((0, 0), (1, 1), (0, 1), (1, 0))):
                                ins = nc.vector.tensor_tensor(tmp[t][0:p, :], pair(j, 512 * a, 512 * a + 512, p), gsp[0:p, f, b, :], ALU.mult)
                                if t < 3:
                                    link(ins)
                                else:
                                    ins.then_inc(S["z_mul"], 1)
                        dve.wait_ge(S["z_skip"], 4 * hf + 4)
                        for i in range(4):
                            j = AT[("Y", hf, i)]
                            dve.wait_ge(S["tile_done"], j + 1)
                            nc.vector.scalar_tensor_tensor(zt_c[:, i, :], full(j), 1.0 / (T * Z_S * F_S * G_S), zt_c[:, i, :],
                                                           ALU.mult, ALU.add).then_inc(S["y_done"], 1)

            dve.wait_ge(S["dec_ln"], 1)
            link(nc.vector.tensor_scalar(dec[:, 16:20], dec[:, 8:12], -1.0, None, ALU.mult))
            dve.wait_ge(S["tables"], 48)
            dve.wait_ge(S["tile_done"], AT[("Y", 1, 3)] + 1)
            for hh in range(HEADS):
                if hh:
                    dve.wait_ge(S["mask_ready"], hh)
                link(nc.vector.tensor_scalar(marg[0][:, :], utab[:, :], 0.0, dec[:, 16 + hh:17 + hh], ALU.max, ALU.mult))
                link(nc.vector.tensor_scalar(marg[1][:, :], utab[:, :], 0.0, dec[:, 12 + hh:13 + hh], ALU.min, ALU.mult))
                nc.vector.tensor_tensor(marg[0][:, :], marg[0][:, :], marg[1][:, :], ALU.add).then_inc(S["mask_arg"], 1)
                if hh == 0:
                    raw_lo(C_Q + 2)
            for i in range(8):
                j = AT[("QK", i)]
                dve.wait_ge(S["tile_done"], j + 1)
                if i:
                    dve.wait_ge(S["rot_ready"], i)
                else:
                    dve.wait_ge(S["u_used"], 24)
                link(nc.vector.tensor_tensor(rot[0][:, :], full(j), cosT[:, :], ALU.mult))
                link(nc.vector.tensor_tensor(rot[1][0:64, :], full(j, 64, 128), sinT[64:128, :], ALU.mult))
                nc.vector.tensor_tensor(rot[1][64:128, :], full(j, 0, 64), sinT[0:64, :], ALU.mult).then_inc(S["rot_mul"], 1)
                if i % 2:
                    if i < 7:
                        raw_lo(C_Q + 2 + i // 2 + 1)
            raw_lo(C_V + 2)
            raw_lo(C_V + 3)
            raw_lo(C_V + 4)
            raw_lo(C_V + 5)
            dve.wait_ge(S["mask_ready"], HEADS)

            def og(hh):
                dve.wait_ge(S["rms_root"], hh + 1)
                link(nc.vector.reciprocal(rs[:, hh, :], rs[:, hh, :]))
                for j2 in range(2):
                    c = 2 * hh + j2
                    nc.vector.scalar_tensor_tensor(qk[:, hh + 4 * j2, :], qk[:, hh + 4 * j2, :], rgs[:, c:c + 1], rs[:, hh, :],
                                                   ALU.mult, ALU.mult).then_inc(S["og_ready"], 1)

            for hh in range(HEADS):
                for k, (s0, p) in enumerate(TS):
                    j = AT[("S", hh, k)]
                    dve.wait_ge(S["tile_done"], j + 1)
                    nc.vector.scalar_tensor_tensor(sc[hh % 2][0:p, k, :], full(j, 0, p), DK ** -0.5,
                                                   mask[0:p, hh, U0 - s0:U0 - s0 + T], ALU.mult, ALU.mult).then_inc(S["sc_ready"], 1)
                if hh >= 2:
                    og(hh - 2)
            og(HEADS - 2)
            og(HEADS - 1)
            for c in range(4):
                raw_lo(C_GR + 2 + c)
                for j in (2 * c, 2 * c + 1):
                    i = j // 2 + 4 * (j % 2)
                    dve.wait_ge(S["silu_ready"], j + 1)
                    dve.wait_ge(S["og_ready"], j + 1)
                    nc.vector.tensor_tensor(tb[j % 2][:, :], sgt[j % 2][:, :], qk[:, i, :], ALU.mult).then_inc(S["yain_prod"], 1)
                    dve.wait_ge(S["yain_hi"], j + 1)
                    nc.vector.tensor_tensor(yain[:, j, 1, :], tb[j % 2][:, :], yain[:, j, 0, :], ALU.subtract).then_inc(S["yain_split"], 1)
            for c in range(4):
                raw_lo(C_A + 2 + 2 * c)
                raw_lo(C_A + 3 + 2 * c)
                for j in (2 * c, 2 * c + 1):
                    dve.wait_ge(S["tile_done"], AT[("YA", j)] + 1)
                    dve.wait_ge(S["gate_ready"], j + 1)
                    nc.vector.scalar_tensor_tensor(mix32[:, j, :], full(AT[("YA", j)]), MIX_S / (W_S * YA_S), sgt[j % 2][:, :],
                                                   ALU.mult, ALU.mult).then_inc(S["mix_a"], 1)
            for c in range(4):
                raw_lo(C_B + 2 + 2 * c)
                raw_lo(C_B + 3 + 2 * c)
                for j in (2 * c, 2 * c + 1):
                    dve.wait_ge(S["tile_done"], AT[("YB", j)] + 1)
                    dve.wait_ge(S["gate_ready"], KD + j + 1)
                    if j >= 2:
                        dve.wait_ge(S["mix_split"], j - 1)
                    nc.vector.scalar_tensor_tensor(tb[j % 2][:, :], full(AT[("YB", j)]), MIX_S / (W_S * YB_S), sgt[j % 2][:, :],
                                                   ALU.mult, ALU.mult).then_inc(S["mix_b"], 1)
                    dve.wait_ge(S["mix_b"], j + 1)
                    nc.vector.tensor_tensor(tb[j % 2][:, :], tb[j % 2][:, :], mix32[:, j, :], ALU.add).then_inc(S["mix_sum"], 1)
                    dve.wait_ge(S["mix_hi"], j + 1)
                    nc.vector.tensor_tensor(mixp[:, j, 1, :], tb[j % 2][:, :], mixp[:, j, 0, :], ALU.subtract).then_inc(S["mix_split"], 1)
            raw_lo(C_O + 2)
            dve.wait_ge(S["h_again"], 32)
            for c in range(4):
                if c == 1:
                    raw_lo(C_O + 3)
                for k, (_, p) in enumerate(TS):
                    j = AT[("WO", c, k)]
                    hc = h[0:p, k, CW * c:CW * c + CW]
                    dve.wait_ge(S["tile_done"], j + 1)
                    nc.vector.scalar_tensor_tensor(hc, pair(j, 0, CW, p), 1.0 / (W_S * MIX_S), hc, ALU.mult, ALU.add).then_inc(S["h_add"], 1)
            dve.wait_ge(S["g_rows"], 32)
            for k, (_, p) in enumerate(TS):
                dve.wait_ge(S["rms2_root"], k + 1)
                link(nc.vector.reciprocal(rinv[0:p, k:k + 1], root[0:p, k:k + 1]))
                dve.wait_ge(S["h_add"], 3 * NT + k + 1)
                nc.vector.scalar_tensor_tensor(xn2[0:p, k, :], h[0:p, k, :], rinv[0:p, k:k + 1], g2b[0:p, :],
                                               ALU.mult, ALU.mult).then_inc(S["xn2_ready"], 1)
            for k, (_, p) in enumerate(TS):
                dve.wait_ge(S["xn2_hi"], k + 1)
                nc.vector.tensor_tensor(xn2p[0:p, k, 1, :], xn2[0:p, k, :], xn2p[0:p, k, 0, :], ALU.subtract).then_inc(S["xn2_lo"], 1)
            link(nc.vector.memset(lgs[:, 0, :], 0.0))
            j = AT[("L",)]
            dve.wait_ge(S["tile_done"], j + 1)
            nc.vector.tensor_copy(lgs[:, 1:NT, :].rearrange("p k e -> p (k e)"), pair(j, E, NT * E)).then_inc(S["logits_in"], 1)
            nc.vector.tensor_copy(lgs[0:NMETA, 0, :], pair(j, 0, E, NMETA)).then_inc(S["logits_in"], 1)
            dve.wait_ge(S["logits_in"], 2)
            link(nc.vector.tensor_reduce(lmax[:, :], lgs[:, :, :], AX_X, ALU.max))
            nc.vector.tensor_tensor(lgs[:, :, :], lgs[:, :, :], lmax[:, :].unsqueeze(2).to_broadcast([128, NT, E]),
                                    ALU.subtract).then_inc(S["lg_sub"], 1)
            dve.wait_ge(S["lg_exp"], 1)
            link(nc.vector.tensor_reduce(lsum[:, :], lgs[:, :, :], AX_X, ALU.add))
            link(nc.vector.reciprocal(lsum[:, :], lsum[:, :]))
            nc.vector.tensor_tensor(lgs[:, :, :], lgs[:, :, :], lsum[:, :].unsqueeze(2).to_broadcast([128, NT, E]),
                                    ALU.mult).then_inc(S["lg_aff"], 1)
            j = AT[("AT",)]
            dve.wait_ge(S["tile_done"], j + 1)
            nc.vector.tensor_copy(work[:, :], full(j, 0, E)).then_inc(S["work_in"], 1)
            dve.wait_ge(S["work_in"], 1)
            for r in range(ROUNDS):
                v8, i8 = vals[:, 8 * r:8 * r + 8], idxu[:, 8 * r:8 * r + 8]
                link(nc.vector.max(v8, work[:, :]))
                link(nc.vector.max_index(i8, v8, work[:, :]))
                if r < ROUNDS - 1:
                    link(nc.vector.match_replace(work[:, :], v8, work[:, :], -1.0))
            nc.vector.tensor_copy(idxf[:, :], idxu[:, :]).then_inc(S["idx_found"], 1)
            dve.wait_ge(S["idx_found"], 1)
            dve.wait_ge(S["moe_consts"], 32)
            nc.vector.tensor_tensor(blki[:, :, :], idxf[:, 0:CAP].unsqueeze(1).to_broadcast([E, E, CAP]),
                                    blk[:, :].rearrange("p (e c) -> p e c", e=E), ALU.mult).then_inc(S["blk_ready"], 1)
            dve.wait_ge(S["xt_evac"], KD)
            dve.wait_ge(S["xn2_lo"], NT)
            nc.vector.memset(xcur[:, :, :], 0.0).then_inc(S["xcur_pad"], 1)
            j = AT[("C",)]
            dve.wait_ge(S["tile_done"], j + 1)
            nc.vector.tensor_copy(cols[:, :], pair(j, 0, 2 * E, CAP)).then_inc(S["cols_in"], 1)
            for i in range(2):
                j = AT[("R", i)]
                dve.wait_ge(S["tile_done"], j + 1)
                nc.vector.tensor_copy(idxb[:, T * i:T * i + T], full(j)).then_inc(S["idx_row"], 1)
            dve.wait_ge(S["cols_in"], 1)
            dve.wait_ge(S["idx_row"], 2)

            def select(e):
                for k, (_, p) in enumerate(TS):
                    nc.vector.tensor_scalar(sel[0:p, k, :], idxb[0:p, bass.ds(e * CAP, CAP)], con[0:p, C_TOK + k:C_TOK + k + 1], None,
                                            ALU.is_equal).then_inc(S["sel_ready"], 1)

            select(0)

            def moe(e, last):
                if not isinstance(e, int) or e:
                    dve.wait_ge(S["scat_done"], e * 4)
                nc.vector.tensor_scalar(st[:, :], iota[0:CAP, NMETA:T], cols[:, bass.ds(e, 1)], cols[:, bass.ds(e + E, 1)],
                                        ALU.is_equal, ALU.mult).then_inc(S["st_ready"], 1)
                if not last:
                    dve.wait_ge(S["xe_done"], e + 1)
                    select(e + 1)
                dve.wait_ge(S["silu_g"], e + 1)
                dve.wait_ge(S["chunk_used"], e * MOE_CH + 8)
                nc.vector.tensor_tensor(hid[:, :, :].rearrange("p g n -> p (g n)"), ps_all[:, 512 * GR:1024 * GR],
                                        hg[:, :, :].rearrange("p g n -> p (g n)"), ALU.mult).then_inc(S["hid_ready"], 1)
                dve.wait_ge(S["chunk_used"], e * MOE_CH + 12)
                for g in range(GR):
                    r = min(32, CAP - 32 * g)
                    for nq in range(2, 4):
                        nc.vector.tensor_copy(ye[32 * g:32 * g + r, 256 * nq:256 * nq + 256],
                                              ps_all[32 * nq:32 * nq + r, 1536 + 512 * g:1792 + 512 * g]).then_inc(S["ye_dve"], 1)
                for k in range(1, NT):
                    dve.wait_ge(S["scat_done"], e * 4 + k)
                    b = (3072, 0)[k % 2]
                    nc.vector.tensor_tensor(h[:, k, :], ps_all[:, b:b + D], h[:, k, :], ALU.add).then_inc(S["moe_add"], 1)

            with dve.Fori(0, E - 1) as e:
                moe(e, False)
            moe(E - 1, True)
            for k in range(1, NT):
                dve.wait_ge(S["fin_root"], k)
                link(nc.vector.reciprocal(rinv[:, k:k + 1], root[:, k:k + 1]))
                dve.wait_ge(S["fin_sq"], k)
                nc.vector.scalar_tensor_tensor(h[:, k, :], h[:, k, :], rinv[:, k:k + 1], gfb[:, :], ALU.mult, ALU.mult).then_inc(S["fin_ready"], 1)

        @block.tensor
        def _(pe):
            def begin(name):
                n = AT[name]
                if n >= 4:
                    _, sem, count = JOBS[n - 4]
                    pe.wait_ge(S[sem], count)
                return n

            def end(ins):
                ins.then_inc(S["tile_done"], 1)

            def wide(n, p, terms):
                for i, (l, r) in enumerate(terms):
                    for a, b, c in ((0, CUT, P0), (CUT, T, 512)):
                        last = nc.tensor.matmul(pair(n, c, c + b - a, p), l, r[:, a:b],
                                                start=i == 0, stop=i == len(terms) - 1)
                return last

            def three(l, r):
                return [(l[0], r[0]), (l[0], r[1]), (l[1], r[0])]

            def project(n, c, i, src):
                ws = wsp[c % 3]
                terms = []
                for k in range(KD):
                    terms += three([ws[:, q, k, 128 * i:128 * i + 128] for q in range(2)], [src[:, k, q, :] for q in range(2)])
                return wide(n, 128, terms)

            def tokens(n, c, k, src):
                s0, p = TS[k]
                ws = wsp[c % 3]
                i = 0
                for kk in range(KD):
                    for l, r in three([src[:, kk, q, s0:s0 + p] for q in range(2)], [ws[:, q, kk, :] for q in range(2)]):
                        last = nc.tensor.matmul(pair(n, 0, CW, p), l, r, start=i == 0, stop=i == 3 * KD - 1)
                        i += 1
                return last

            def chunk(c):
                pe.wait_ge(S["raw_lo"], c + 1)
                pe.wait_ge(S["raw_hi"], c + 1)

            def filt(l):
                if l == 0:
                    pe.wait_ge(S["filt_params"], 48)
                    n = begin(("H", 0))
                    end(wide(n, 64, [(fpar[0:33, F_W1:F_W1 + 64], feat[:, :])]))
                else:
                    pe.wait_ge(S["sin_ready"], l)
                    n = begin(("H", l))
                    f = (F_W1, F_W2, F_W3)[l]
                    end(wide(n, 64, [(fpar[:, f:f + 64], hdn[:, :])]))

            filt(0)
            pe.wait_ge(S["consts"], 48)
            for j in range(KD):
                n = begin(("X", j))
                pe.wait_ge(S["hs_ready"], NT)
                for k, (s0, p) in enumerate(TS):
                    c = P0 + s0
                    last = nc.tensor.transpose(pair(n, c, c + p), htok[0:p, k, 128 * j:128 * j + 128], ident[0:p, 0:p])
                end(last)
            pe.wait_ge(S["x_split"], KD)
            pe.wait_ge(S["x_hi"], KD)
            for hf in range(2):
                for part in range(3):
                    for i in range(4):
                        c = 6 * hf + 2 * part + i // 2
                        chunk(c)
                        n = begin(("U", hf, part, i))
                        end(project(n, c, i % 2, xnt))
                        if hf == 0 and part == 0 and i in (1, 3):
                            filt((i + 1) // 2)
                    if part == 0:
                        pe.wait_ge(S["sin_ready"], 3)
                        for k, (s0, p) in enumerate(TS):
                            n = begin(("FL", hf, k))
                            for a in range(2):
                                last = nc.tensor.matmul(pair(n, 512 * a, 512 * a + 512, p), hdn[:, s0:s0 + p],
                                                        w4[:, D * a + HALF * hf:D * a + HALF * hf + HALF], start=True, stop=True)
                            end(last)
                    if part != 1:
                        continue

                    def spectrum(n, f, srcs):
                        f0, fp = TS[f]
                        for a in range(2):
                            i = 0
                            for k, (s0, p) in enumerate(TS):
                                for l, r in three([dft_f[0:p, k, 2 * a + q, f0:f0 + fp] for q in range(2)],
                                                  [srcs[a][0:p, k, q, :] for q in range(2)]):
                                    last = nc.tensor.matmul(pair(n, 512 * a, 512 * a + 512, fp), l, r, start=i == 0, stop=i == 3 * NT - 1)
                                    i += 1
                        return last

                    pe.wait_ge(S["dft_fwd"], 16)
                    pe.wait_ge(S["filt_lo"], 2 * NT * (hf + 1))
                    pe.wait_ge(S["filt_hi"], 2 * NT * (hf + 1))
                    for f in range(NT):
                        n = begin(("G", hf, f))
                        end(spectrum(n, f, (fp_, fm_)))
                    pe.wait_ge(S["u_used"], 12 * hf + 8)
                    for k, (s0, p) in enumerate(TS):
                        n = begin(("ZT", hf, k))
                        for i in range(4):
                            last = nc.tensor.transpose(pair(n, 128 * i, 128 * i + 128, p), zt_c[:, i, s0:s0 + p], ident[:, :])
                        end(last)
                    pe.wait_ge(S["zt_split"], NT * (hf + 1))
                    pe.wait_ge(S["zt_hi"], NT * (hf + 1))
                    for f in range(NT):
                        n = begin(("Z", hf, f))
                        end(spectrum(n, f, (zt_t, zt_t)))
                    pe.wait_ge(S["dft_inv"], 16)
                    pe.wait_ge(S["p_lo"], 2 * NT * (hf + 1))
                    pe.wait_ge(S["p_hi"], 2 * NT * (hf + 1))
                    for i in range(4):
                        n = begin(("Y", hf, i))
                        terms = []
                        for f, (_, fp) in enumerate(TS):
                            for a in range(2):
                                terms += three([psp[0:fp, f, 2 * a + q, 128 * i:128 * i + 128] for q in range(2)],
                                               [dft_i[0:fp, f, 2 * a + q, :] for q in range(2)])
                        end(wide(n, 128, terms))
            for i in range(8):
                chunk(C_Q + i // 2)
                n = begin(("QK", i))
                end(project(n, C_Q + i // 2, i % 2, xnt))
            for c in range(4):
                chunk(C_V + c)
                for k in range(NT):
                    n = begin(("V", c, k))
                    end(tokens(n, C_V + c, k, xnt))
            pe.wait_ge(S["rot_ready"], 8)
            for hh in range(HEADS + 1):
                if hh < HEADS:
                    for k, (s0, p) in enumerate(TS):
                        n = begin(("S", hh, k))
                        end(wide(n, p, [(qk[:, 4 + hh, s0:s0 + p], qk[:, hh, :])]))
                if hh >= 1:
                    g = hh - 1
                    pe.wait_ge(S["sc_ready"], NT * hh)
                    pe.wait_ge(S["v_evac"], 4 * NT)
                    for j2 in range(2):
                        n = begin(("O", g, j2))
                        c = DV * g + 128 * j2
                        end(wide(n, 128, [(v[0:p, k, c:c + 128], sc[g % 2][0:p, k, :]) for k, (_, p) in enumerate(TS)]))
                    n = begin(("N", g))
                    pe.wait_ge(S["sq_ready"], 4 * hh)
                    pe.wait_ge(S["border"], 5)
                    end(wide(n, 128, [(ones[:, :], sqb[:, j2, :]) for j2 in range(2)]))
            for j in range(KD):
                chunk(C_GR + j // 2)
                n = begin(("GR", j))
                end(project(n, C_GR + j // 2, j % 2, xnt))
            pe_in = {"A": ("yain", yain, C_A), "B": ("yb", ybin, C_B)}
            for key, (what, src, c0) in pe_in.items():
                for c in range(4):
                    chunk(c0 + 2 * c)
                    for i in range(2):
                        n = begin(("G" + key, 2 * c + i))
                        end(project(n, c0 + 2 * c, i, xnt))
                    if c == 0:
                        if key == "A":
                            pe.wait_ge(S["yain_split"], KD)
                            pe.wait_ge(S["yain_hi"], KD)
                        else:
                            pe.wait_ge(S["u_used"], 24)
                            pe.wait_ge(S["yb_hi"], KD)
                    chunk(c0 + 2 * c + 1)
                    for i in range(2):
                        n = begin(("Y" + key, 2 * c + i))
                        end(project(n, c0 + 2 * c + 1, i, src))
            pe.wait_ge(S["mix_split"], KD)
            pe.wait_ge(S["mix_hi"], KD)
            for c in range(4):
                chunk(C_O + c)
                for k in range(NT):
                    n = begin(("WO", c, k))
                    end(tokens(n, C_O + c, k, mixp))
            pe.wait_ge(S["xn2_ready"], NT)
            for j in range(KD):
                n = begin(("XT", j))
                for k, (s0, p) in enumerate(TS):
                    last = nc.tensor.transpose(pair(n, P0 + s0, P0 + s0 + p), xn2[0:p, k, 128 * j:128 * j + 128], ident[0:p, 0:p])
                end(last)
            n = begin(("L",))
            pe.wait_ge(S["xt_evac"], KD)
            for k, (s0, p) in enumerate(TS):
                for j in range(KD):
                    last = nc.tensor.matmul(pair(n, E * k, E * k + E, p), xn2t[:, j, s0:s0 + p], par[:, C_WR + E * j:C_WR + E * j + E],
                                            start=j == 0, stop=j == KD - 1)
            end(last)
            n = begin(("AT",))
            pe.wait_ge(S["lg_aff"], 1)
            for k, (s0, p) in enumerate(TS):
                last = nc.tensor.transpose(pair(n, P0 + s0, P0 + s0 + p, E), lgs[0:p, k, :], ident[0:p, 0:p])
            end(last)
            n = begin(("C",))
            pe.wait_ge(S["idx_found"], 1)
            for a, src in enumerate((idxf, vals)):
                last = nc.tensor.transpose(pair(n, E * a, E * a + E, CAP), src[:, 0:CAP], ident[0:E, 0:E])
            end(last)
            pe.wait_ge(S["blk_ready"], 1)
            flat = blki[:, :, :].rearrange("p e c -> p (e c)")
            for i in range(2):
                n = begin(("R", i))
                end(wide(n, 128, [(ones[0:E, :], flat[:, T * i:T * i + T])]))
            pe.wait_ge(S["idx_row"], 2)

            def gather(e):
                pe.wait_ge(S["sel_ready"], (e + 1) * NT)
                for kk in range(KD):
                    c = 3072 + 512 * (kk // 4) + CAP * (kk % 4)
                    for k, (_, p) in enumerate(TS):
                        for q in range(2):
                            last = nc.tensor.matmul(ps_all[:, c:c + CAP], xn2p[0:p, k, q, kk:kk + KD * 127 + 1:KD], sel[0:p, k, :],
                                                    start=k == 0 and q == 0, stop=k == NT - 1 and q == 1)
                last.then_inc(S["xe_done"], 1)

            pe.wait_ge(S["xn2_lo"], NT)
            pe.wait_ge(S["xn2_hi"], NT)
            gather(0)

            def moe(e, last_one):
                later = not isinstance(e, int) or e
                pe.wait_ge(S["xcur_ready"], e * 2 + 2)
                if later:
                    pe.wait_ge(S["moe_add"], e * 4)
                for c in range(MOE_CH):
                    if c == 4 and later:
                        pe.wait_ge(S["ye_act"], e * 2 * GR)
                        pe.wait_ge(S["ye_dve"], e * 2 * GR)
                    if c == 8:
                        if not last_one:
                            gather(e + 1)
                        pe.wait_ge(S["hid_ready"], e + 1)
                        for g in range(GR):
                            for s in range(4):
                                last = nc.tensor.transpose(ps_all[:, 512 * g + 128 * s:512 * g + 128 * s + 128],
                                                           hid[:, g, s:s + 4 * 127 + 1:4], ident[:, :])
                        last.then_inc(S["hidt_done"], 1)
                        pe.wait_ge(S["hidt_ready"], e + 1)
                    pe.wait_ge(slot_in[c % SLOTS], e * 32 + 16 * (c // SLOTS + 1))
                    ws = moe_dst(c)
                    if c < 8:
                        for kk in range(2):
                            k = 2 * (c % 4) + kk
                            for g in range(GR):
                                b = 512 * (GR * (c // 4) + g)
                                for j in range(4):
                                    last = nc.tensor.matmul(ps_all[32 * j:32 * j + 32, b:b + 512], xcur[:, k, 32 * g:32 * g + 32],
                                                            ws[:, kk, 512 * j:512 * j + 512], start=k == 0, stop=k == KD - 1)
                    else:
                        j = c - 8
                        for s in range(4):
                            for g in range(GR):
                                b = 1536 + 512 * g
                                for nq in range(4):
                                    last = nc.tensor.matmul(ps_all[32 * nq:32 * nq + 32, b:b + 256], hidt[:, g, s, 32 * j:32 * j + 32],
                                                            ws[:, s, 256 * nq:256 * nq + 256], start=j == 0 and s == 0, stop=j == 3 and s == 3)
                    last.then_inc(S["chunk_used"], 1)
                pe.wait_ge(S["ye_act"], e * 2 * GR + 2 * GR)
                pe.wait_ge(S["ye_dve"], e * 2 * GR + 2 * GR)
                pe.wait_ge(S["st_ready"], e + 1)
                if not last_one:
                    pe.wait_ge(S["xcur_ready"], e * 2 + 4)
                for k in range(1, NT):
                    b = (3072, 0)[k % 2]
                    if k > 2:
                        pe.wait_ge(S["moe_add"], e * 4 + k - 2)
                    for n in range(2):
                        last = nc.tensor.matmul(ps_all[:, b + 512 * n:b + 512 * n + 512], st[:, 128 * (k - 1):128 * k],
                                                ye[:, 512 * n:512 * n + 512], start=True, stop=True)
                    last.then_inc(S["scat_done"], 1)

            moe(0, False)
            with pe.Fori(1, E - 1) as e:
                moe(e, False)
            moe(E - 1, True)


def shape_tables():
    import numpy as np
    f32 = np.float32

    def tiles(a):
        o = np.zeros((128, NT) + a.shape[1:], a.dtype)
        for k, (s0, p) in enumerate(TS):
            o[:p, k] = a[s0:s0 + p]
        return o

    th = 2 * np.pi * (np.arange(T) + 0.5) / (2 * T)
    ang = np.outer(np.arange(T), th)
    parts = []
    for a in (np.cos(ang), np.sin(ang)):
        hi = a.astype(np.float16)
        parts += [hi, (a - hi).astype(np.float16)]
    fwd = tiles(np.stack(parts, 1))
    inv = tiles(np.stack([p.T for p in parts], 1))
    t = np.arange(T, dtype=f32)
    tn = t / f32(T - 1)
    max_decay, min_decay = np.log(1e-2) / 0.3, np.log(1e-2) / 1.5
    deltas = np.abs(np.linspace(min_decay, max_decay, D)).astype(f32)
    wnd = (np.exp(-(tn[:, None] * deltas[None, :]).astype(np.float64)) * F_S).astype(f32)
    bands = 16
    fr = np.linspace(1e-4, bands - 1, bands).astype(f32)
    fa = ((f32(2 * np.pi) * t / f32(T))[:, None] * fr[None, :]).astype(f32).astype(np.float64)
    feat = np.concatenate([tn[:, None], np.cos(fa), -np.sin(fa)], 1).astype(f32).T
    half = DK // 2
    inv_f = (10000.0 ** (-(np.arange(half, dtype=f32) / f32(half)).astype(np.float64))).astype(f32)
    ra = (t[:, None] * inv_f[None, :]).astype(f32).astype(np.float64).T
    cos, sin = np.cos(ra) / W_S, np.sin(ra) / W_S
    con = np.zeros((128, N_CON), f32)
    for k, (s0, p) in enumerate(TS):
        con[:, C_TOK + k] = s0 + np.arange(128)
    con[:, C_EPS] = EPS
    return {
        "c_dft_f": fwd, "c_dft_i": inv,
        "c_win": tiles(wnd.reshape(T, 2, HALF)),
        "c_feat": feat, "c_con": con, "c_ident": np.eye(128, dtype=f32),
        "c_cos": np.concatenate([cos, cos]).astype(f32),
        "c_sin": np.concatenate([sin, -sin]).astype(f32),
        "c_u": (np.arange(UW)[None, :] - U0 - np.arange(128)[:, None]).astype(f32),
        "c_iota": np.broadcast_to(np.arange(T, dtype=f32), (128, T)),
        "c_blk": np.repeat(np.eye(E, dtype=f32), CAP, 1),
    }


def kernel(**inputs):
    import numpy as np
    import concourse.bacc as bacc
    from concourse import mybir as mb
    from concourse.bass_utils import run_bass_kernel_spmd as run

    a = {k: np.asarray(x) for k, x in inputs.items()}

    def by_feature(x):
        return x.reshape(-1, 128).T

    f32 = np.float32
    p_par = np.concatenate(
        [by_feature(a["norm1_g"][0]), by_feature(a["ret_head_norm_g"][0])]
        + [by_feature(a["hy_conv_w"][0, t]) for t in range(3)]
        + [by_feature(a["hy_conv_b"][0]), by_feature(a["hy_skip"][0]),
           np.broadcast_to(a["ret_decay_fwd"], (128, HEADS)), np.broadcast_to(a["ret_decay_bwd"], (128, HEADS)),
           a["w_router"][0].reshape(KD, 128, E).transpose(1, 0, 2).reshape(128, KD * E)], 1)
    w1 = np.zeros((64, 64), f32)
    w1[:33] = a["hy_filt_w1"][0]
    p_filt = np.concatenate([w1, a["hy_filt_w2"][0], a["hy_filt_w3"][0]]
                            + [a[n][0][:, None] for n in ("hy_filt_b1", "hy_filt_b2", "hy_filt_b3", "hy_filt_freq")], 1)
    arrays = {n: a[n] for n in ("x", "meta_tokens", "w_in", "w_ret_out", "hy_filt_w4", "w_hy_out", "w_o", "norm2_g",
                                "w_exp_gate", "w_exp_up", "w_exp_down", "final_norm_g")}
    arrays.update(shape_tables())
    arrays.update(p_par=p_par, p_filt=p_filt)
    nc = bacc.Bacc("TRN2", target_bir_lowering=False, num_devices=1)
    feeds, aps = {}, {}
    for n, x in arrays.items():
        x = np.ascontiguousarray(x)
        feeds[f"in_{n}"] = x
        aps[n] = nc.dram_tensor(f"in_{n}", x.shape, mb.dt.from_np(x.dtype), kind="ExternalInput").ap()
    out = nc.dram_tensor("out", (1, SEQ, D), F32, kind="ExternalOutput").ap()
    build(nc, aps, out)
    r = run(nc, [feeds], core_ids=[0])
    return r.results[0]["out"]
```
